# Optimizing a Trainium2 kernel written in Bass

```python
import jax
import jax.numpy as jnp
from jax import lax

D_MODEL = 1024
BATCH = 1
SEQ = 256
DEPTH = 2

ATTN_HEADS = 8
HEAD_DIM = 64
ATTN_WIDTH = ATTN_HEADS * HEAD_DIM
POOL_WINDOWS = (2, 4, 8, 16)
POOL_GROUPS = len(POOL_WINDOWS)
POOL_GROUP_DIM = 64
POOL_WIDTH = POOL_GROUPS * POOL_GROUP_DIM
HGRN_HEADS = 4
HGRN_HEAD_DIM = 64
HGRN_WIDTH = HGRN_HEADS * HGRN_HEAD_DIM
MIX_WIDTH = ATTN_WIDTH + POOL_WIDTH + HGRN_WIDTH
SPLIT_SIZES = (ATTN_WIDTH, ATTN_WIDTH, ATTN_WIDTH, POOL_WIDTH, HGRN_WIDTH, HGRN_WIDTH, HGRN_WIDTH, HGRN_WIDTH)
IN_WIDTH = sum(SPLIT_SIZES)
D_FF = 2816
MOBA_BLOCK = 256
MOBA_TOPK = 3
MOBA_Q_CHUNK = 64
HGRN_CHUNK = 64
ROPE_THETA = 10000.0
EPS = 1e-6
NEG_INF = -1e30
LB_FLOOR = 1e-20

kernel_name = 'hybrid_moba_pool_hgrn2_macaron'

def rms_norm(x, gain):
    x32 = x.astype(jnp.float32)
    y = x32 * lax.rsqrt(jnp.mean(x32 * x32, axis=-1, keepdims=True) + EPS)
    return (y * gain.astype(jnp.float32)).astype(x.dtype)

def swiglu(h, w_gate, w_up, w_down):
    return (jax.nn.silu(h @ w_gate) * (h @ w_up)) @ w_down

def apply_rope(x, pos):
    half = x.shape[-1] // 2
    inv_freq = ROPE_THETA ** (-jnp.arange(half, dtype=jnp.float32) / half)
    ang = pos.astype(jnp.float32)[:, None] * inv_freq[None, :]
    cos, sin = jnp.cos(ang), jnp.sin(ang)
    x32 = x.astype(jnp.float32)
    x1, x2 = x32[..., :half], x32[..., half:]
    return jnp.concatenate([x1 * cos - x2 * sin, x2 * cos + x1 * sin], axis=-1).astype(x.dtype)

def moba_attention(q, k, v):
    b, h, s, dh = q.shape
    nb = -(-s // MOBA_BLOCK)
    pad = nb * MOBA_BLOCK - s
    widths = ((0, 0), (0, 0), (0, pad), (0, 0))
    k_blocks = jnp.pad(k, widths).reshape(b, h, nb, MOBA_BLOCK, dh)
    v_blocks = jnp.pad(v, widths).reshape(b, h, nb, MOBA_BLOCK, dh)
    k_mean = jnp.mean(k_blocks.astype(jnp.float32), axis=3)
    n_sel = min(MOBA_TOPK, nb - 1)
    scale = dh ** -0.5
    n_chunks = s // MOBA_Q_CHUNK
    q_chunks = q.reshape(b, h, n_chunks, MOBA_Q_CHUNK, dh).transpose(2, 0, 1, 3, 4)
    b_idx = jnp.arange(b)[:, None, None, None]
    h_idx = jnp.arange(h)[None, :, None, None]
    key_off = jnp.arange(MOBA_BLOCK)
    q_off = jnp.arange(MOBA_Q_CHUNK)
    blk_ids = jnp.arange(nb)

    def chunk(args):
        q_c, c = args
        q_pos = c * MOBA_Q_CHUNK + q_off
        own = (c * MOBA_Q_CHUNK) // MOBA_BLOCK
        k_own = lax.dynamic_index_in_dim(k_blocks, own, axis=2, keepdims=False)
        v_own = lax.dynamic_index_in_dim(v_blocks, own, axis=2, keepdims=False)
        s_own = jnp.einsum('bhqd,bhkd->bhqk', q_c, k_own).astype(jnp.float32) * scale
        s_own = jnp.where(own * MOBA_BLOCK + key_off[None, :] <= q_pos[:, None], s_own, NEG_INF)
        if n_sel == 0:
            p = jax.nn.softmax(s_own, axis=-1).astype(v.dtype)
            return jnp.einsum('bhqk,bhkd->bhqd', p, v_own)
        gate = jnp.einsum('bhqd,bhnd->bhqn', q_c.astype(jnp.float32), k_mean)
        gate = jnp.where(blk_ids < own, gate, NEG_INF)
        _, sel = lax.top_k(gate, n_sel)
        sel_ok = jnp.arange(n_sel) < own
        k_sel = k_blocks[b_idx, h_idx, sel]
        v_sel = v_blocks[b_idx, h_idx, sel]
        s_sel = jnp.einsum('bhqd,bhqnkd->bhqnk', q_c, k_sel).astype(jnp.float32) * scale
        s_sel = jnp.where(sel_ok[:, None], s_sel, NEG_INF)
        n_keys = n_sel * MOBA_BLOCK
        scores = jnp.concatenate([s_sel.reshape(b, h, MOBA_Q_CHUNK, n_keys), s_own], axis=-1)
        p = jax.nn.softmax(scores, axis=-1).astype(v.dtype)
        p_sel = p[..., :n_keys].reshape(b, h, MOBA_Q_CHUNK, n_sel, MOBA_BLOCK)
        out = jnp.einsum('bhqnk,bhqnkd->bhqd', p_sel, v_sel)
        return out + jnp.einsum('bhqk,bhkd->bhqd', p[..., n_keys:], v_own)

    out = lax.map(chunk, (q_chunks, jnp.arange(n_chunks)))
    return out.transpose(1, 2, 0, 3, 4).reshape(b, h, s, dh)

def multiscale_pool(u, pool_w, pool_scale):
    b, s, _ = u.shape
    u32 = u.astype(jnp.float32)
    csum = jnp.pad(jnp.cumsum(u32, axis=1), ((0, 0), (1, 0), (0, 0)))
    count = jnp.arange(1, s + 1, dtype=jnp.float32)
    diffs = []
    for g, w in enumerate(POOL_WINDOWS):
        sl = slice(g * POOL_GROUP_DIM, (g + 1) * POOL_GROUP_DIM)
        cg = csum[..., sl]
        lo = jnp.pad(cg[:, :s + 1 - w], ((0, 0), (w - 1, 0), (0, 0)))
        mean = (cg[:, 1:] - lo) / jnp.minimum(count, float(w))[None, :, None]
        diffs.append(mean - u32[..., sl])
    d = jnp.stack(diffs, axis=2)
    y = jnp.einsum('bsgc,gce->bsge', d, pool_w.astype(jnp.float32)).reshape(b, s, POOL_WIDTH)
    return (y * pool_scale.astype(jnp.float32)).astype(u.dtype)

def hgrn2(q, f_logit, i, gate, lower_bound, out_norm):
    b, s, _ = q.shape
    n_c = s // HGRN_CHUNK
    z = f_logit.astype(jnp.float32)
    lb = lower_bound.astype(jnp.float32)
    log_f = jnp.logaddexp(jnp.log(jnp.maximum(lb, LB_FLOOR)), jnp.log1p(-lb) + jax.nn.log_sigmoid(z))
    key = (1.0 - lb) * jax.nn.sigmoid(-z)
    query = jax.nn.silu(q.astype(jnp.float32)) * HGRN_HEAD_DIM ** -0.5
    value = i.astype(jnp.float32)

    def chunks(t):
        return t.reshape(b, n_c, HGRN_CHUNK, HGRN_HEADS, HGRN_HEAD_DIM).transpose(1, 0, 3, 2, 4)

    causal = jnp.tril(jnp.ones((HGRN_CHUNK, HGRN_CHUNK), dtype=bool))[:, :, None]

    def step(state, inp):
        q_c, k_c, v_c, g_c = inp
        cum = jnp.cumsum(g_c, axis=2)
        last = cum[:, :, -1]
        o_inter = jnp.einsum('bhtk,bhkv->bhtv', q_c * jnp.exp(cum), state)
        diff = cum[:, :, :, None, :] - cum[:, :, None, :, :]
        decay = jnp.where(causal, jnp.exp(jnp.minimum(diff, 0.0)), 0.0)
        scores = jnp.einsum('bhtk,bhsk,bhtsk->bhts', q_c, k_c, decay)
        o_intra = jnp.einsum('bhts,bhsv->bhtv', scores, v_c)
        k_dec = k_c * jnp.exp(last[:, :, None, :] - cum)
        state = jnp.exp(last)[..., None] * state + jnp.einsum('bhsk,bhsv->bhkv', k_dec, v_c)
        return state, o_inter + o_intra

    state0 = jnp.zeros((b, HGRN_HEADS, HGRN_HEAD_DIM, HGRN_HEAD_DIM), jnp.float32)
    _, o = lax.scan(step, state0, (chunks(query), chunks(key), chunks(value), chunks(log_f)))
    o = o.transpose(1, 0, 3, 2, 4).reshape(b, s, HGRN_HEADS, HGRN_HEAD_DIM)
    g = gate.astype(jnp.float32).reshape(b, s, HGRN_HEADS, HGRN_HEAD_DIM)
    y = rms_norm(o, out_norm) * jax.nn.silu(g)
    return y.reshape(b, s, HGRN_WIDTH).astype(q.dtype)

def token_mixing(h, w_in, q_norm, k_norm, pool_w, pool_scale, lower_bound, hgrn_out_norm, w_out, pos):
    b, s, _ = h.shape
    proj = h @ w_in
    offsets = []
    acc = 0
    for sz in SPLIT_SIZES[:-1]:
        acc += sz
        offsets.append(acc)
    q_a, k_a, v_a, u_p, q_h, f_h, i_h, g_h = jnp.split(proj, offsets, axis=-1)

    def heads(t):
        return t.reshape(b, s, ATTN_HEADS, HEAD_DIM).transpose(0, 2, 1, 3)

    q = apply_rope(rms_norm(heads(q_a), q_norm), pos)
    k = apply_rope(rms_norm(heads(k_a), k_norm), pos)
    y_attn = moba_attention(q, k, heads(v_a)).transpose(0, 2, 1, 3).reshape(b, s, ATTN_WIDTH)
    y_pool = multiscale_pool(u_p, pool_w, pool_scale)
    y_hgrn = hgrn2(q_h, f_h, i_h, g_h, lower_bound, hgrn_out_norm)
    y = jnp.concatenate([y_attn, y_pool, y_hgrn], axis=-1)
    return y @ w_out

def setup_inputs(seed: int = 0) -> dict:
    key = jax.random.key(seed)
    ks = jax.random.split(key, 18)
    f32 = jnp.float32

    def normal(k, shape, scale):
        return jax.random.normal(k, shape, f32) * scale

    def gain(k, shape):
        return 1.0 + 0.05 * jax.random.normal(k, shape, f32)

    return {
        'x': normal(ks[0], (BATCH, SEQ, D_MODEL), 1.0),
        'ffn1_norm': gain(ks[1], (DEPTH, D_MODEL)),
        'ffn1_w_gate': normal(ks[2], (DEPTH, D_MODEL, D_FF), D_MODEL ** -0.5),
        'ffn1_w_up': normal(ks[3], (DEPTH, D_MODEL, D_FF), D_MODEL ** -0.5),
        'ffn1_w_down': normal(ks[4], (DEPTH, D_FF, D_MODEL), D_FF ** -0.5),
        'mix_norm': gain(ks[5], (DEPTH, D_MODEL)),
        'w_in': normal(ks[6], (DEPTH, D_MODEL, IN_WIDTH), D_MODEL ** -0.5),
        'q_norm': gain(ks[7], (DEPTH, HEAD_DIM)),
        'k_norm': gain(ks[8], (DEPTH, HEAD_DIM)),
        'pool_w': normal(ks[9], (DEPTH, POOL_GROUPS, POOL_GROUP_DIM, POOL_GROUP_DIM), POOL_GROUP_DIM ** -0.5),
        'pool_scale': gain(ks[10], (DEPTH, POOL_WIDTH)),
        'hgrn_lb': normal(ks[11], (DEPTH, HGRN_WIDTH), 0.5),
        'hgrn_out_norm': gain(ks[12], (DEPTH, HGRN_HEAD_DIM)),
        'w_out': normal(ks[13], (DEPTH, MIX_WIDTH, D_MODEL), MIX_WIDTH ** -0.5),
        'ffn2_norm': gain(ks[14], (DEPTH, D_MODEL)),
        'ffn2_w_gate': normal(ks[15], (DEPTH, D_MODEL, D_FF), D_MODEL ** -0.5),
        'ffn2_w_up': normal(ks[16], (DEPTH, D_MODEL, D_FF), D_MODEL ** -0.5),
        'ffn2_w_down': normal(ks[17], (DEPTH, D_FF, D_MODEL), D_FF ** -0.5),
    }

def reference(x, ffn1_norm, ffn1_w_gate, ffn1_w_up, ffn1_w_down, mix_norm, w_in, q_norm, k_norm,
              pool_w, pool_scale, hgrn_lb, hgrn_out_norm, w_out, ffn2_norm, ffn2_w_gate, ffn2_w_up,
              ffn2_w_down):
    pos = jnp.arange(x.shape[1])
    lb_soft = jax.nn.softmax(hgrn_lb.astype(jnp.float32), axis=0)
    lower_bounds = jnp.concatenate([jnp.zeros_like(lb_soft[:1]), jnp.cumsum(lb_soft[:-1], axis=0)], axis=0)
    for l in range(DEPTH):
        x = x + 0.5 * swiglu(rms_norm(x, ffn1_norm[l]), ffn1_w_gate[l], ffn1_w_up[l], ffn1_w_down[l])
        x = x + token_mixing(rms_norm(x, mix_norm[l]), w_in[l], q_norm[l], k_norm[l], pool_w[l],
                             pool_scale[l], lower_bounds[l], hgrn_out_norm[l], w_out[l], pos)
        x = x + 0.5 * swiglu(rms_norm(x, ffn2_norm[l]), ffn2_w_gate[l], ffn2_w_up[l], ffn2_w_down[l])
    return x


_drawn_inputs = setup_inputs


def setup_inputs(seed=0):
    import zlib

    import numpy as np

    out = dict(_drawn_inputs(seed))
    spreads = {}
    factors = {'q_norm': 7.207, 'k_norm': 7.035, 'hgrn_lb': 2.684, 'hgrn_out_norm': 3.417}
    for name, (base, spread) in spreads.items():
        noise = np.random.default_rng([zlib.crc32(name.encode()), seed]).standard_normal(out[name].shape)
        drawn = base * np.exp(spread * noise) if base else spread * noise
        out[name] = jnp.asarray(drawn.astype(out[name].dtype))
    for name, factor in factors.items():
        out[name] = (out[name] * factor).astype(out[name].dtype)
    return out
```

```python
from contextlib import ExitStack

import numpy as np

import concourse.bass as bass
from concourse import mybir
from concourse.alu_op_type import AluOpType as ALU

F32 = mybir.dt.float32
F32R = mybir.dt.float32r
BF16 = mybir.dt.bfloat16
I32 = mybir.dt.int32
U16 = mybir.dt.uint16
ACT = mybir.ActivationFunctionType
AX = mybir.AxisListType.X

P = 128
SEQ, D, DEPTH, FF = 256, 1024, 2, 2816
TILES = SEQ // P
KT = D // P
FT = FF // P
HEADS, HD = 8, 64
ATTN = HEADS * HD
POOL_WINDOWS = (2, 4, 8, 16)
POOL, HGRN, HH = 256, 256, 4
IN_WIDTH = 3 * ATTN + POOL + 4 * HGRN
EPS = 1e-6
NEG = -1e30
LB_FLOOR = 1e-20
THETA = 10000.0

BLOCK = 4096
UNIT = BLOCK // 2
CHUNK = 256
CHUNKS = FF // CHUNK
DOWN = -(-FT // 4)
B_FFN1 = 0
B_DOWN1 = B_FFN1 + CHUNKS
B_IN = B_DOWN1 + DOWN
B_OUT = B_IN + 6
B_FFN2 = B_OUT + 2
B_DOWN2 = B_FFN2 + CHUNKS
BLOCKS = B_DOWN2 + DOWN
UNITS = 2 * BLOCKS
assert BLOCKS % 2 == 0 and CHUNKS % 2 == 1
RAW = 4
QF, IG, QA, KA, VA, UP = range(6)
IN_COLS = [(3 * ATTN + POOL, 512), (3 * ATTN + POOL + 512, 512), (0, 512), (512, 512), (1024, 512), (3 * ATTN, POOL)]

LEVELS = [0, 32, 16, 8, 4, 2, 1, 64, 128]
PACKED = 7
LN_SHIFT = 40
BAND0 = P + 16

GU = 0
TR = 2
DN = 4


class Signal:

    def __init__(self, sem, per_layer, start=0):
        self.sem, self.per, self.start = sem, per_layer, start

    def at(self, l, n):
        return l * self.per + (self.start + n)


class Chain:

    def __init__(self, steps, eng, l):
        self.steps, self.eng, self.l, self.n = steps, eng, l, 0

    def step(self, ins):
        self.n += 1
        ins.then_inc(self.steps.sem, 1)
        self.eng.wait_ge(self.steps.sem, self.steps.at(self.l, self.n))


def bc(ap, axis, shape):
    return ap.unsqueeze(axis).to_broadcast(shape)


def build(nc, a, out):
    ctx = ExitStack()
    with ctx:
        base = (nc.sbuf_base + 31) // 32 * 32
        cursor = [base]

        def place(name, shape, dt=F32, at=None):
            size = int(np.prod(shape[1:])) * {F32: 4, F32R: 4, BF16: 2, I32: 4}[dt]
            if at is None:
                at = cursor[0]
                cursor[0] += (size + 31) // 32 * 32
            return nc.alloc_sbuf_tensor_at(name, shape, dt, offset=at), at

        raw, _ = place("raw", [P, RAW, UNIT])
        whi, _ = place("whi", [P, 2, BLOCK], F32R)
        wlo, _ = place("wlo", [P, 2, BLOCK], F32R)
        x, _ = place("x", [P, TILES, D])
        xn, xn_at = place("xn", [P, TILES, D])
        hT_hi, _ = place("hT_hi", [P, KT, SEQ], F32R)
        hT_lo, _ = place("hT_lo", [P, KT, SEQ], F32R)
        gain, _ = place("gain", [P, D])
        ident, _ = place("ident", [P, P])
        ident16, _ = place("ident16", [P, P], BF16)
        causal16, _ = place("causal16", [P, P], BF16)
        levmask, _ = place("levmask", [P, PACKED, 64], I32)
        scan_keep, _ = place("scan_keep", [P, 2 * SEQ], BF16)
        band0, _ = place("band0", [P, 4, BAND0])
        band1, _ = place("band1", [P, 4, P])
        trig, _ = place("trig", [P, TILES, 2, HD])
        rgain, _ = place("rgain", [P, DEPTH, 5, HD])
        lbt, _ = place("lbt", [P, DEPTH, 2])
        lbf, _ = place("lbf", [P, DEPTH, 2])
        oml, _ = place("oml", [P, DEPTH, 2])
        lbin, _ = place("lbin", [P, 2, DEPTH, 2])
        lbe, _ = place("lbe", [P, 8])
        halfneg, _ = place("halfneg", [P, 8])
        ss, _ = place("ss", [P, TILES, 2])
        var, _ = place("var", [P, TILES])
        rstd, _ = place("rstd", [P, TILES])
        hss, _ = place("hss", [P, 5, 8])
        hvar, _ = place("hvar", [P, 5, 8])
        hrs, _ = place("hrs", [P, 5, 8])
        scl, _ = place("scl", [P, TILES, 8])
        mx, _ = place("mx", [P, TILES, 8])
        nb, _ = place("nb", [P, TILES, 8])
        rows, _ = place("rows", [P, TILES, 8])
        rinv, _ = place("rinv", [P, TILES, 8])

        arena = cursor[0]
        act_hi, _ = place("act_hi", [P, FT, SEQ], F32R)
        act_lo, _ = place("act_lo", [P, FT, SEQ], F32R)
        ffn_end = cursor[0]
        cursor[0] = arena
        fsig, fsig_at = place("fsig", [P, 2 * SEQ])
        small, _ = place("small", [P, 2 * SEQ])
        key, _ = place("key", [P, 2 * SEQ])
        qry, _ = place("qry", [P, 2 * SEQ])
        pc, _ = place("pc", [P, 2 * SEQ])
        dec, _ = place("dec", [P, 2, 2 * SEQ])
        kl, _ = place("kl", [P, 2, 2 * SEQ])
        ql, _ = place("ql", [P, 2, 2 * SEQ])
        sp, _ = place("sp", [P, 8, 64])
        st, _ = place("st", [P, 8, P])
        s128, _ = place("s128", [P, 4, P])
        ig, _ = place("ig", [P, TILES, 512])
        qk, qk_at = place("qk", [P, 2, TILES, 512])
        rtmp, rtmp_at = place("rtmp", [P, 512])
        vv, _ = place("vv", [P, TILES, 512])
        qkT, _ = place("qkT", [P, 2, 4, SEQ])
        pT, _ = place("pT", [P, 2, 512])
        cursor[0] = max(cursor[0], ffn_end)
        assert cursor[0] <= nc.sbuf_usable_end, cursor[0] - nc.sbuf_usable_end
        qf, _ = place("qf", [P, TILES, 512], at=qk_at)
        p0, _ = place("p0", [P, 8, P], at=fsig_at)
        p1, _ = place("p1", [P, 8, SEQ], at=qk_at)
        dT, _ = place("dT", [P, 2, SEQ], at=rtmp_at)
        gs, _ = place("gs", [P, 2 * SEQ], at=xn_at)
        osq, _ = place("osq", [P, 2 * SEQ], at=xn_at + 2048)
        ya, _ = place("ya", [P, TILES, 512], at=xn_at + 4096)
        un, _ = place("un", [P, TILES, POOL], at=xn_at + 4096)

        ps = ctx.enter_context(nc.psum_tensor("ps", [P, 8, 512], F32))

        def signal(name, per, start=0):
            return Signal(ctx.enter_context(nc.semaphore(name)), per, start)

        consts_in = signal("consts_in", 0)
        lb_in = signal("lb_in", 0)
        x_in = [signal(f"x_in{t}", 0) for t in range(TILES)]
        ident_in = signal("ident_in", 0)
        gain_in = signal("gain_in", 3 * 16)
        raw_in = [signal(f"raw_in{i}", UNITS // RAW * 32) for i in range(RAW)]
        out_done = signal("out_done", 0)
        passed = signal("passed", 0)
        poolw_zero = signal("poolw_zero", 0)
        lb_exp = signal("lb_exp", 0)
        setup_v = signal("setup_v", 0)
        ready_v = signal("ready_v", 0)
        hi_ready = signal("hi_ready", UNITS)
        lo_ready = signal("lo_ready", UNITS, RAW)
        unit_used = signal("unit_used", UNITS, 4)
        resid = signal("resid", 12, 12)
        sq_ready = signal("sq_ready", 6)
        var_ready = signal("var_ready", 6)
        rstd_ready = signal("rstd_ready", 6)
        xn_ready = signal("xn_ready", 6, 6)
        xT_done = signal("xT_done", 12)
        hhi_ready = signal("hhi_ready", 12)
        hlo_ready = signal("hlo_ready", 12)
        gu_done = signal("gu_done", 2 * CHUNKS)
        gate_ready = signal("gate_ready", 4 * CHUNKS)
        prod_ready = signal("prod_ready", 4 * CHUNKS, 2)
        aT_done = signal("aT_done", 4 * CHUNKS)
        ahi_ready = signal("ahi_ready", 4 * CHUNKS)
        alo_ready = signal("alo_ready", 4 * CHUNKS, 2)
        dn_done = signal("dn_done", 3)
        proj_done = signal("proj_done", 6)
        proj_out = signal("proj_out", 12)
        clear_done = signal("clear_done", 1)
        qfT_done = signal("qfT_done", 2)
        sig_ready = signal("sig_ready", 2)
        gsig_ready = signal("gsig_ready", 1)
        f_ready = signal("f_ready", 1)
        ln_ready = signal("ln_ready", 1)
        pc_ready = signal("pc_ready", 1)
        kq_ready = signal("kq_ready", 9)
        dif_ready = signal("dif_ready", 8)
        dec_ready = signal("dec_ready", 8)
        lev_done = signal("lev_done", 9)
        lev_out = signal("lev_out", 7)
        lev_out_a = signal("lev_out_a", 2)
        st_ready = signal("st_ready", 2)
        gate_done = signal("gate_done", 1)
        hsq_ready = signal("hsq_ready", 5)
        hsum_done = signal("hsum_done", 5)
        hvar_ready = signal("hvar_ready", 5)
        hrs_ready = signal("hrs_ready", 5)
        rope_ready = signal("rope_ready", 4)
        qkT_done = signal("qkT_done", 4)
        qkT_out_a = signal("qkT_out_a", 2)
        qkT_out_v = signal("qkT_out_v", 2)
        s_done = signal("s_done", 3)
        nb_ready = signal("nb_ready", 3)
        exp_done = signal("exp_done", 3)
        dT_done = signal("dT_done", 1)
        dT_out = signal("dT_out", 1)
        yp_done = signal("yp_done", 1)
        yp_hi = signal("yp_hi", 1)
        yp_lo = signal("yp_lo", 1)
        ho_done = signal("ho_done", 1)
        yh_ready = signal("yh_ready", 1)
        yhT_done = signal("yhT_done", 1)
        yh_hi = signal("yh_hi", 1)
        yh_lo = signal("yh_lo", 1)
        pT_done = signal("pT_done", 3)
        pT_a = signal("pT_a", 3)
        pT_v = signal("pT_v", 3)
        pv_done = signal("pv_done", 3)
        ya_ready = signal("ya_ready", 2)
        yaT_done = signal("yaT_done", 2)
        ya_hi = signal("ya_hi", 2)
        ya_lo = signal("ya_lo", 2)
        vchain = signal("vchain", V_STEPS)
        pchain = signal("pchain", P_STEPS)

        def slot(block):
            return block % 2

        def tok(t):
            return slice(t * P, (t + 1) * P)

        def half(n):
            return slice(n * 512, (n + 1) * 512)

        def plain_wait(eng):
            eng.sem_inc(passed.sem, 1)

        def chunk_pairs(eng):
            return eng.Fori(0, (CHUNKS - 1) // 2)

        def load_unit(sp_, l, block, h, src, cols, pair=0):
            u = 2 * block + h
            s = u % RAW
            sp_.wait_ge(lo_ready.sem, l * UNITS + pair * 4 + (u + 1))
            plain_wait(sp_)
            for dst, view in src(raw[:, s, 0:cols]):
                sp_.dma_start(dst, view).then_inc(raw_in[s].sem, 16)

        def split_hi(act, l, block, h, cols=UNIT, pair=0):
            u = 2 * block + h
            s = u % RAW
            act.wait_ge(raw_in[s].sem, l * raw_in[s].per + pair * 32 + 32 * (u // RAW + 1))
            act.wait_ge(unit_used.sem, l * UNITS + pair * 4 + (u + 1))
            at = h * cols
            act.activation(whi[:, slot(block), at:at + cols], raw[:, s, 0:cols], ACT.Copy).then_inc(hi_ready.sem, 1)

        def split_lo(dve, l, block, h, cols=UNIT, pair=0):
            u = 2 * block + h
            at = h * cols
            w = slot(block)
            dve.wait_ge(hi_ready.sem, l * UNITS + pair * 4 + (u + 1))
            dve.tensor_tensor(wlo[:, w, at:at + cols], raw[:, u % RAW, 0:cols],
                              whi[:, w, at:at + cols].bitcast(F32), ALU.subtract).then_inc(lo_ready.sem, 1)

        def unit_cols(block):
            short = block in (B_DOWN1 + DOWN - 1, B_DOWN2 + DOWN - 1, B_IN + UP)
            return UNIT // 2 if short else UNIT

        def split_block(split, eng, l, block):
            for h in range(2):
                split(eng, l, block, h, unit_cols(block))

        def unit_ready(pe, l, block, h, pair=0):
            pe.wait_ge(lo_ready.sem, l * UNITS + pair * 4 + (RAW + 2 * block + h + 1))

        def products(pe, outs, a_hi, a_lo, w, cols, first, last):
            for n, o in enumerate(outs):
                pe.matmul(o, a_hi, whi[:, w, cols[n]:cols[n] + 512], start=first, stop=False)
            for n, o in enumerate(outs):
                pe.matmul(o, a_hi, wlo[:, w, cols[n]:cols[n] + 512], start=False, stop=False)
            for n, o in enumerate(outs):
                mm = pe.matmul(o, a_lo, whi[:, w, cols[n]:cols[n] + 512], start=False, stop=last)
            return mm

        def first_products(pe, l, block, n, t, o, width):
            w = slot(block)
            for g in range(2):
                if t == 0:
                    pe.wait_ge(hi_ready.sem, hi_ready.at(l, 2 * block + g + 1))
                pe.wait_ge(hhi_ready.sem, hhi_ready.at(l, 4 * n + 2 * t + g + 1))
                for kt in range(4 * g, 4 * g + 4):
                    pe.matmul(o, hT_hi[:, kt, tok(t)], whi[:, w, kt * width:(kt + 1) * width], start=kt == 0, stop=False)
            for g in range(2):
                if t == 0:
                    unit_ready(pe, l, block, g)
                for kt in range(4 * g, 4 * g + 4):
                    pe.matmul(o, hT_hi[:, kt, tok(t)], wlo[:, w, kt * width:(kt + 1) * width], start=False, stop=False)
                pe.wait_ge(hlo_ready.sem, hlo_ready.at(l, 4 * n + 2 * t + g + 1))
                for kt in range(4 * g, 4 * g + 4):
                    mm = pe.matmul(o, hT_lo[:, kt, tok(t)], whi[:, w, kt * width:(kt + 1) * width], start=False,
                                   stop=kt == KT - 1)
                if t == 1:
                    mm.then_inc(unit_used.sem, 1)
            return mm

        def norm_squares(act, l, n, t):
            for hf in range(2):
                if n == 0:
                    act.wait_ge(resid.sem, l * 12 + (8 + 2 * t + hf + 1))
                else:
                    act.wait_ge(resid.sem, resid.at(l, (n - 1) * 4 + 2 * t + hf + 1))
                ins = act.activation(xn[:, t, half(hf)], x[:, t, half(hf)], ACT.Square, accum_out=ss[:, t, hf:hf + 1])
            ins.then_inc(sq_ready.sem, 1)

        def norm_rows(dve, chain, l, n, t):
            dve.wait_ge(sq_ready.sem, sq_ready.at(l, 2 * n + t + 1))
            chain.step(dve.tensor_scalar(var[:, t:t + 1], ss[:, t, 0:1], ss[:, t, 1:2], 1.0 / D, ALU.add, ALU.mult))
            dve.tensor_scalar(var[:, t:t + 1], var[:, t:t + 1], EPS, None, ALU.add).then_inc(var_ready.sem, 1)
            dve.wait_ge(rstd_ready.sem, rstd_ready.at(l, 2 * n + t + 1))
            if t == 0:
                dve.wait_ge(gain_in.sem, gain_in.at(l, 16 * (n + 1)))
            dve.scalar_tensor_tensor(xn[:, t, :], x[:, t, :], rstd[:, t:t + 1], gain[:, :], ALU.mult,
                                     ALU.mult).then_inc(xn_ready.sem, 1)

        def norm_rstd(pool, l, n, t):
            pool.wait_ge(var_ready.sem, var_ready.at(l, 2 * n + t + 1))
            pool.tensor_tensor(rstd[:, t:t + 1], var[:, t:t + 1], halfneg[:, 0:1], ALU.pow).then_inc(rstd_ready.sem, 1)

        def norm_transpose(pe, l, n, t, bank):
            pe.wait_ge(xn_ready.sem, xn_ready.at(l, 2 * n + t + 1))
            for g in range(2):
                if t == 1:
                    pe.wait_ge(hlo_ready.sem, hlo_ready.at(l, 4 * n + g + 1))
                for j in range(4):
                    mm = pe.transpose(ps[:, bank + g, j * P:(j + 1) * P], xn[:, t, (4 * g + j) * P:(4 * g + j + 1) * P],
                                      ident[:, :])
                mm.then_inc(xT_done.sem, 1)

        def bank_view(bank, lo=0, n=512, inner=P):
            return ps[:, bank, lo:lo + n].rearrange("p (j t) -> p j t", t=inner)

        def norm_hi(act, l, n, t, bank):
            for g in range(2):
                act.wait_ge(xT_done.sem, xT_done.at(l, 4 * n + 2 * t + g + 1))
                act.activation(hT_hi[:, 4 * g:4 * g + 4, tok(t)], bank_view(bank + g), ACT.Copy).then_inc(hhi_ready.sem, 1)

        def norm_lo(dve, l, n, t, bank):
            for g in range(2):
                dve.wait_ge(hhi_ready.sem, hhi_ready.at(l, 4 * n + 2 * t + g + 1))
                dve.tensor_tensor(hT_lo[:, 4 * g:4 * g + 4, tok(t)], bank_view(bank + g),
                                  hT_hi[:, 4 * g:4 * g + 4, tok(t)].bitcast(F32), ALU.subtract).then_inc(hlo_ready.sem, 1)

        def add_residual(dve, l, stage_no, t, banks, factor):
            if t == 0:
                dve.wait_ge(dn_done.sem, dn_done.at(l, stage_no + 1))
            else:
                last = (B_DOWN1 + DOWN, B_OUT + 2, B_DOWN2 + DOWN)[stage_no]
                dve.wait_ge(unit_used.sem, unit_used.at(l, 2 * last))
            for hf in range(2):
                dve.scalar_tensor_tensor(x[:, t, half(hf)], ps[:, banks[t][hf], :], factor, x[:, t, half(hf)], ALU.mult,
                                         ALU.add).then_inc(resid.sem, 1)

        DN_FFN = ((DN, DN + 1), (DN + 2, DN + 3))
        DN_MIX = ((6, 7), (2, 3))

        def idx(f, c, t):
            return 2 * CHUNKS * f + 2 * c + t

        def chunk_products(pe, l, f, c, t, pair=0):
            block = (B_FFN1, B_FFN2)[f] + c
            n = idx(f, c, t)
            pe.wait_ge(prod_ready.sem, l * 4 * CHUNKS + pair * 4 + (n + 1))
            for h in range(2):
                if t == 0:
                    unit_ready(pe, l, block, h, pair)
                for k in range(4):
                    kt = 4 * h + k
                    mm = products(pe, [ps[:, GU + t, :]], hT_hi[:, kt, tok(t)], hT_lo[:, kt, tok(t)], slot(block),
                                  [kt * 512], kt == 0, kt == KT - 1)
                if t == 1:
                    mm.then_inc(unit_used.sem, 1)
            if t == 0:
                mm.then_inc(gu_done.sem, 1)

        def chunk_transpose(pe, l, f, c, t, pair=0):
            n = idx(f, c, t)
            pe.wait_ge(prod_ready.sem, l * 4 * CHUNKS + pair * 4 + (2 + n + 1))
            pe.wait_ge(alo_ready.sem, l * 4 * CHUNKS + pair * 4 + (n + 1))
            for j in range(2):
                mm = pe.transpose(ps[:, TR + t, j * P:(j + 1) * P], xn[:, t, j * P:(j + 1) * P], ident[:, :])
            mm.then_inc(aT_done.sem, 1)

        def chunk_gate(act, l, f, c, t, pair=0):
            block = (B_FFN1, B_FFN2)[f] + c
            if t == 0:
                act.wait_ge(gu_done.sem, l * 2 * CHUNKS + pair * 2 + (CHUNKS * f + c + 1))
            else:
                act.wait_ge(unit_used.sem, l * UNITS + pair * 4 + (4 + 2 * block + 2))
            act.activation(xn[:, t, CHUNK:2 * CHUNK], ps[:, GU + t, 0:CHUNK], ACT.Silu).then_inc(gate_ready.sem, 1)

        def chunk_hi(act, l, f, c, t, pair=0):
            n = idx(f, c, t)
            act.wait_ge(aT_done.sem, l * 4 * CHUNKS + pair * 4 + (n + 1))
            first = 2 * c + 4 * pair
            act.activation(act_hi[:, bass.ds(first, 2), tok(t)], bank_view(TR + t, 0, CHUNK),
                           ACT.Copy).then_inc(ahi_ready.sem, 1)

        def chunk_product(dve, l, f, c, t, pair=0):
            n = idx(f, c, t)
            dve.wait_ge(gate_ready.sem, l * 4 * CHUNKS + pair * 4 + (n + 1))
            dve.tensor_tensor(xn[:, t, 0:CHUNK], xn[:, t, CHUNK:2 * CHUNK], ps[:, GU + t, CHUNK:2 * CHUNK],
                              ALU.mult).then_inc(prod_ready.sem, 1)

        def chunk_lo(dve, l, f, c, t, pair=0):
            n = idx(f, c, t)
            dve.wait_ge(ahi_ready.sem, l * 4 * CHUNKS + pair * 4 + (n + 1))
            first = 2 * c + 4 * pair
            dve.tensor_tensor(act_lo[:, bass.ds(first, 2), tok(t)], bank_view(TR + t, 0, CHUNK),
                              act_hi[:, bass.ds(first, 2), tok(t)].bitcast(F32), ALU.subtract).then_inc(alo_ready.sem, 1)

        def down_products(pe, l, f, j, t, arrive, done, finish=False, halves=(0, 1)):
            block = (B_DOWN1, B_DOWN2)[f] + j
            per = unit_cols(block) // D
            for h in halves:
                if arrive:
                    unit_ready(pe, l, block, h)
                for k in range(per):
                    at = h * per + k
                    kt = 4 * j + at
                    mm = products(pe, [ps[:, DN_FFN[t][n], :] for n in range(2)], act_hi[:, kt, tok(t)],
                                  act_lo[:, kt, tok(t)], slot(block), [at * D, at * D + 512], kt == 0, kt == FT - 1)
                if done:
                    mm.then_inc(unit_used.sem, 1)
            if finish:
                mm.then_inc(dn_done.sem, 1)

        def ffn_tensor(pe, l, f):
            block = (B_FFN1, B_FFN2)[f]
            for t in range(TILES):
                if t == 1:
                    norm_transpose(pe, l, 2 * f, 1, TR if f == 0 else 4)
                pe.wait_ge(prod_ready.sem, prod_ready.at(l, idx(f, 0, t) - 1))
                mm = first_products(pe, l, block, 2 * f, t, ps[:, GU + t, :], 512)
                if t == 0:
                    mm.then_inc(gu_done.sem, 1)
            chunk_transpose(pe, l, f, 0, 0)
            with chunk_pairs(pe) as i:
                for e in range(2):
                    chunk_products(pe, l, f, 1 + e, 0, i)
                    chunk_transpose(pe, l, f, e, 1, i)
                    chunk_products(pe, l, f, 1 + e, 1, i)
                    chunk_transpose(pe, l, f, 1 + e, 0, i)
            for j in range(DOWN - 2):
                if j < DOWN - 2:
                    pe.wait_ge(alo_ready.sem, alo_ready.at(l, idx(f, min(2 * j + 1, CHUNKS - 1), 1) + 1))
                down_products(pe, l, f, j, 0, True, False)
                if j == 0:
                    chunk_transpose(pe, l, f, CHUNKS - 1, 1)
                down_products(pe, l, f, j, 1, False, True)
            pe.wait_ge(alo_ready.sem, alo_ready.at(l, idx(f, CHUNKS - 1, 1) + 1))
            for j in range(DOWN - 2, DOWN):
                down_products(pe, l, f, j, 0, True, False, j == DOWN - 1)
            down_products(pe, l, f, DOWN - 2, 1, False, True)
            if f == 0:
                norm_transpose(pe, l, 1, 0, TR)
            down_products(pe, l, f, DOWN - 1, 1, False, True)

        def ffn_side(eng, l, f, split, first_step, second_step):
            b0 = (B_FFN1, B_FFN2)[f]
            for t in range(TILES):
                split(eng, l, b0 + 1, t)
                first_step(eng, l, f, 0, t)
            second_step(eng, l, f, 0, 0)
            with chunk_pairs(eng) as i:
                for e in range(2):
                    for h in range(2):
                        split(eng, l, b0 + 2 + e, h, UNIT, i)
                    first_step(eng, l, f, 1 + e, 0, i)
                    second_step(eng, l, f, e, 1, i)
                    first_step(eng, l, f, 1 + e, 1, i)
                    second_step(eng, l, f, 1 + e, 0, i)
            bd = (B_DOWN1, B_DOWN2)[f]
            split_block(split, eng, l, bd + 1)
            second_step(eng, l, f, CHUNKS - 1, 1)
            for j in range(2, DOWN):
                split_block(split, eng, l, bd + j)

        assert unit_cols(B_DOWN1) == UNIT and unit_cols(B_DOWN2) == UNIT

        def norm_tail_scalar(act, l, n, block, bank):
            norm_squares(act, l, n, 0)
            split_hi(act, l, block, 0)
            norm_hi(act, l, n, 0, bank)
            split_hi(act, l, block, 1)
            norm_squares(act, l, n, 1)
            norm_hi(act, l, n, 1, bank)

        def norm_tail_vector(dve, chain, l, n, block, bank, banks, factor):
            add_residual(dve, l, n - 1, 0, banks, factor)
            norm_rows(dve, chain, l, n, 0)
            split_lo(dve, l, block, 0)
            norm_lo(dve, l, n, 0, bank)
            add_residual(dve, l, n - 1, 1, banks, factor)
            split_lo(dve, l, block, 1)
            norm_rows(dve, chain, l, n, 1)
            norm_lo(dve, l, n, 1, bank)

        PROJ = ((0, 1), (4, 5), (6, 7), (0, 1), (4, 5), (6, 7))

        def proj_products(pe, l, part, t, between=None):
            block = B_IN + part
            width = IN_COLS[part][1]
            if part >= 3:
                pe.wait_ge(proj_out.sem, proj_out.at(l, 2 * (part - 3) + t + 1))
            for h in range(2):
                if h == 1 and between:
                    between()
                if t == 0:
                    unit_ready(pe, l, block, h)
                for k in range(4):
                    kt = 4 * h + k
                    o = ps[:, PROJ[part][t], 0:width]
                    w = slot(block)
                    cols = slice(kt * width, (kt + 1) * width)
                    pe.matmul(o, hT_hi[:, kt, tok(t)], whi[:, w, cols], start=kt == 0, stop=False)
                    pe.matmul(o, hT_hi[:, kt, tok(t)], wlo[:, w, cols], start=False, stop=False)
                    mm = pe.matmul(o, hT_lo[:, kt, tok(t)], whi[:, w, cols], start=False, stop=kt == KT - 1)
                if t == 1:
                    mm.then_inc(unit_used.sem, 1)
            if t == 0:
                mm.then_inc(proj_done.sem, 1)

        def proj_wait(eng, l, part, t):
            if t == 0:
                eng.wait_ge(proj_done.sem, proj_done.at(l, part + 1))
            else:
                eng.wait_ge(unit_used.sem, unit_used.at(l, 2 * (B_IN + part) + 2))

        def head_rows(h):
            return slice(64 * (h % 2), 64 * (h % 2) + 64)

        def level_products(pe, l, v):
            b = LEVELS[v]
            pe.wait_ge(kq_ready.sem, kq_ready.at(l, v + 1))
            if 1 <= v <= PACKED:
                pe.wait_ge(lev_out.sem, lev_out.at(l, v))
            if v == PACKED + 1:
                pe.wait_ge(proj_out.sem, proj_out.at(l, 2 * KA + 2))
            plain_wait(pe)
            for h in range(HH):
                r, hh, bank = head_rows(h), h // 2, (TR if v <= PACKED else 0) + h % 2
                ks = (key if b == 0 else kl[:, v % 2, :])[r, hh * SEQ:(hh + 1) * SEQ]
                qs = (qry if b == 0 else ql[:, v % 2, :])[r, hh * SEQ:(hh + 1) * SEQ]
                if b <= 32:
                    for c in range(4):
                        at = (2 * hh + c // 2) * 64
                        mm = pe.matmul(ps[64 * (c % 2):64 * (c % 2) + 64, bank, at:at + 64], ks[:, c * 64:c * 64 + 64],
                                       qs[:, c * 64:c * 64 + 64], start=True, stop=True)
                elif b == 64:
                    for t in range(TILES):
                        at = (2 * hh + t) * 64
                        mm = pe.matmul(ps[0:64, bank, at:at + 64], ks[:, t * P:t * P + 64], qs[:, t * P + 64:(t + 1) * P],
                                       start=True, stop=True)
                else:
                    mm = pe.matmul(ps[:, bank, hh * P:(hh + 1) * P], ks[:, 0:P], qs[:, P:SEQ], start=True, stop=True)
            mm.then_inc(lev_done.sem, 1)

        def s_bank(t, h):
            par, hh = h % 2, h // 2
            if t == 0:
                return 4 + par, hh * P
            return (6 if hh < 2 else 2) + par, (hh % 2) * SEQ

        def mix_tensor(pe, l):
            pe.wait_ge(consts_in.sem, 16 * N_CONSTS)
            first_products(pe, l, B_IN, 1, 0, ps[:, PROJ[QF][0], :], 512).then_inc(proj_done.sem, 1)
            norm_transpose(pe, l, 1, 1, TR)
            first_products(pe, l, B_IN, 1, 1, ps[:, PROJ[QF][1], :], 512)

            def qf_transpose():
                pe.wait_ge(proj_out.sem, proj_out.at(l, 2))
                for which in (1, 0):
                    for ft in range(2):
                        for t in range(TILES):
                            mm = pe.transpose(ps[:, TR + which, ft * SEQ + t * P:ft * SEQ + (t + 1) * P],
                                              qf[:, t, which * 256 + ft * P:which * 256 + (ft + 1) * P], ident[:, :])
                    mm.then_inc(qfT_done.sem, 1)

            proj_products(pe, l, IG, 0, qf_transpose)
            proj_products(pe, l, IG, 1)
            for part in (QA, KA, VA, UP):
                for t in range(TILES):
                    proj_products(pe, l, part, t)
                    level_products(pe, l, 2 * (part - QA) + t)
            level_products(pe, l, 8)

            for w in range(2):
                for t in range(TILES):
                    bank = (2, 3, 0, 1)[2 * w + t]
                    pe.wait_ge(rope_ready.sem, rope_ready.at(l, 2 * w + t + 1))
                    if t == 0:
                        pe.wait_ge(lev_out_a.sem, lev_out_a.at(l, w + 1))
                    for j in range(4):
                        mm = pe.transpose(ps[:, bank, j * P:(j + 1) * P], qk[:, w, t, j * P:(j + 1) * P], ident[:, :])
                    mm.then_inc(qkT_done.sem, 1)

            pe.wait_ge(qkT_out_a.sem, qkT_out_a.at(l, 2))
            pe.wait_ge(qkT_out_v.sem, qkT_out_v.at(l, 2))
            pe.wait_ge(proj_out.sem, proj_out.at(l, 12))
            def scores(t, heads):
                keys = (t + 1) * P
                for h in heads:
                    bank, at = s_bank(t, h)
                    pe.matmul(ps[:, bank, at:at + keys], qkT[head_rows(h), 0, h // 2, tok(t)],
                              qkT[head_rows(h), 1, h // 2, 0:keys], start=True, stop=True)
                    mm = pe.matmul(ps[:, bank, at + t * P:at + keys], ident16[:, :], causal16[:, :], start=False, stop=True,
                                   skip_group_check=True)
                mm.then_inc(s_done.sem, 1)

            scores(0, range(HEADS))

            pe.wait_ge(st_ready.sem, st_ready.at(l, 2))
            for t in range(TILES):
                for h in range(HH):
                    o = ps[:, 1, t * 256 + h * 64:t * 256 + (h + 1) * 64]
                    mm = pe.matmul(o, st[:, 4 * (h % 2) + 2 * (h // 2) + t, :], ig[:, t, h * 64:(h + 1) * 64], start=True,
                                   stop=t == 0)
                    if t == 1:
                        mm = pe.matmul(o, s128[:, 2 * (h % 2) + h // 2, :], ig[:, 0, h * 64:(h + 1) * 64], start=False,
                                       stop=True)
            mm.then_inc(ho_done.sem, 1)

            for g in range(4):
                rows_ = slice(64 * (g % 2), 64 * (g % 2) + 64)
                at = (g // 2) * SEQ
                pe.matmul(ps[rows_, 0, at:at + BAND0], un[:, 0, g * 64:(g + 1) * 64], band0[:, g, :], start=g < 2,
                          stop=False, skip_group_check=True)
                mm = pe.matmul(ps[rows_, 0, at + P:at + SEQ], un[:, 1, g * 64:(g + 1) * 64], band1[:, g, :], start=False,
                               stop=True, skip_group_check=True)
            mm.then_inc(dT_done.sem, 1)

            scores(1, range(0, 4))

            pe.wait_ge(yh_ready.sem, yh_ready.at(l, 1))
            for ft in range(2):
                for t in range(TILES):
                    mm = pe.transpose(ps[:, 1, ft * SEQ + t * P:ft * SEQ + (t + 1) * P],
                                      osq[:, t * 256 + ft * P:t * 256 + (ft + 1) * P], ident[:, :])
            mm.then_inc(yhT_done.sem, 1)
            pe.wait_ge(dT_out.sem, dT_out.at(l, 1))
            pe.wait_ge(poolw_in.sem, poolw_in.at(l, 4 * 16))
            for g2 in range(2):
                mm = pe.matmul(ps[:, 0, g2 * SEQ:(g2 + 1) * SEQ], pool_now[:, g2, :], dT[:, g2, :], start=True, stop=True)
            mm.then_inc(yp_done.sem, 1)

            scores(1, range(4, HEADS))
            pe.wait_ge(exp_done.sem, exp_done.at(l, 1))
            probs_transpose(pe, l, 0)

            pe.wait_ge(yp_lo.sem, yp_lo.at(l, 1))
            pe.wait_ge(yh_lo.sem, yh_lo.at(l, 1))
            pe.wait_ge(exp_done.sem, exp_done.at(l, 2))
            out_products(pe, l, 0, 0)
            probs_values(pe, l, 0)
            pe.wait_ge(exp_done.sem, exp_done.at(l, 3))
            probs_transpose(pe, l, 1)
            out_products(pe, l, 0, 1)
            probs_values(pe, l, 1)
            probs_transpose(pe, l, 2)
            y_transpose(pe, l, 0)
            probs_values(pe, l, 2)
            pe.wait_ge(ya_lo.sem, ya_lo.at(l, 1))
            out_products(pe, l, 1, 0, (0,))
            y_transpose(pe, l, 1)
            out_products(pe, l, 1, 0, (1,)).then_inc(dn_done.sem, 1)
            pe.wait_ge(ya_lo.sem, ya_lo.at(l, 2))
            out_products(pe, l, 1, 1, between=lambda: norm_transpose(pe, l, 2, 0, 4))

        def batch(n, j):
            if n == 0:
                return j, 0
            return 4 * (n - 1) + j % 4, j // 4

        def probs_transpose(pe, l, n):
            if n > 0:
                pe.wait_ge(pT_a.sem, pT_a.at(l, n))
                pe.wait_ge(pT_v.sem, pT_v.at(l, n))
            for j in range(8):
                h, kt = batch(n, j)
                src = p0[:, h, :] if n == 0 else p1[:, h, kt * P:(kt + 1) * P]
                mm = pe.transpose(ps[:, 4 + j // 4, (j % 4) * P:(j % 4 + 1) * P], src, ident[:, :])
            mm.then_inc(pT_done.sem, 1)

        def probs_values(pe, l, n):
            pe.wait_ge(pT_a.sem, pT_a.at(l, n + 1))
            pe.wait_ge(pT_v.sem, pT_v.at(l, n + 1))
            for h in (range(8) if n == 0 else range(4 * (n - 1), 4 * n)):
                tiles = 1 if n == 0 else 2
                for kt in range(tiles):
                    j = h if n == 0 else h - 4 * (n - 1) + 4 * kt
                    mm = pe.matmul(ps[:, min(n, 1), h * HD:(h + 1) * HD], pT[:, j // 4, (j % 4) * P:(j % 4 + 1) * P],
                                   vv[:, kt, h * HD:(h + 1) * HD], start=kt == 0, stop=kt == tiles - 1)
            mm.then_inc(pv_done.sem, 1)

        def y_transpose(pe, l, t):
            pe.wait_ge(ya_ready.sem, ya_ready.at(l, t + 1))
            for j in range(4):
                mm = pe.transpose(ps[:, t, j * P:(j + 1) * P], ya[:, t, j * P:(j + 1) * P], ident[:, :])
            mm.then_inc(yaT_done.sem, 1)

        def out_products(pe, l, j, t, halves=(0, 1), between=None):
            block = B_OUT + j
            for h in halves:
                if t == 0:
                    unit_ready(pe, l, block, h)
                for k in range(2):
                    if between and (h, k) == (1, 1):
                        between()
                    at = 2 * h + k
                    kt = at + (4 if j == 0 else 0)
                    mm = products(pe, [ps[:, DN_MIX[t][n], :] for n in range(2)], hT_hi[:, kt, tok(t)],
                                  hT_lo[:, kt, tok(t)], slot(block), [at * D, at * D + 512], j == 0 and at == 0,
                                  j == 1 and at == 3)
                if t == 1:
                    mm.then_inc(unit_used.sem, 1)
            return mm

        def level_halves(ap, b):
            v = ap.rearrange("p (n j) -> p n j", j=2 * b)
            return v[:, :, 0:b], v[:, :, b:2 * b]

        def proj_copy(act, l, part, t, dst):
            proj_wait(act, l, part, t)
            act.activation(dst, ps[:, PROJ[part][t], 0:IN_COLS[part][1]], ACT.Copy).then_inc(proj_out.sem, 1)

        def level_decay(act, l, v):
            act.wait_ge(dif_ready.sem, dif_ready.at(l, v))
            left, right = level_halves(dec[:, v % 2, :], LEVELS[v])
            act.activation(left, left, ACT.Exp, scale=-1.0)
            act.activation(right, right, ACT.Exp).then_inc(dec_ready.sem, 1)

        def mix_scalar(act, l):
            split_block(split_hi, act, l, B_IN + 1)
            proj_copy(act, l, QF, 0, qf[:, 0, :])
            proj_copy(act, l, QF, 1, qf[:, 1, :])
            split_block(split_hi, act, l, B_IN + 2)
            proj_copy(act, l, IG, 0, ig[:, 0, :])
            act.wait_ge(qfT_done.sem, qfT_done.at(l, 2))
            act.activation(fsig[:, :], ps[:, TR + 1, :], ACT.Sigmoid).then_inc(sig_ready.sem, 1)
            act.activation(key[:, :], ps[:, TR + 1, :], ACT.Sigmoid, scale=-1.0)
            act.activation(qry[:, :], ps[:, TR, :], ACT.Sigmoid).then_inc(sig_ready.sem, 1)
            proj_copy(act, l, IG, 1, ig[:, 1, :])
            act.wait_ge(proj_out.sem, proj_out.at(l, 4))
            act.activation(gs[:, :].rearrange("p (t c) -> p t c", t=2), ig[:, :, 256:512],
                           ACT.Sigmoid).then_inc(gsig_ready.sem, 1)
            act.wait_ge(f_ready.sem, f_ready.at(l, 1))
            act.activation(fsig[:, :], fsig[:, :], ACT.Ln).then_inc(ln_ready.sem, 1)
            split_block(split_hi, act, l, B_IN + 3)
            level_decay(act, l, 1)
            n = 0
            for part in (QA, KA, VA, UP):
                for t in range(TILES):
                    v = 2 * (part - QA) + t
                    if part in (QA, KA):
                        proj_wait(act, l, part, t)
                        if n > 0:
                            act.wait_ge(hsum_done.sem, hsum_done.at(l, n))
                        n += 1
                        act.activation(osq[:, :], ps[:, PROJ[part][t], :], ACT.Square).then_inc(hsq_ready.sem, 1)
                        proj_copy(act, l, part, t, qk[:, part - QA, t, :])
                    elif part == VA:
                        proj_copy(act, l, part, t, vv[:, t, :])
                    else:
                        proj_copy(act, l, part, t, un[:, t, :])
                    if v + 2 <= PACKED + 1:
                        level_decay(act, l, v + 2)
                    if part < UP:
                        split_hi(act, l, B_IN + part + 2, t, unit_cols(B_IN + part + 2))
            act.wait_ge(clear_done.sem, clear_done.at(l, 1))
            act.wait_ge(lev_done.sem, lev_done.at(l, 8))
            act.activation(st[0:64, :, 64:P].rearrange("p (b n) t -> p b n t", b=2),
                           ps[0:64, TR:TR + 2, 0:256].rearrange("p b (n t) -> p b n t", t=64),
                           ACT.Copy).then_inc(lev_out_a.sem, 1)
            act.wait_ge(lev_done.sem, lev_done.at(l, 9))
            act.activation(s128[:, :, :].rearrange("p (b n) t -> p b (n t)", b=2), ps[:, 0:2, 0:256],
                           ACT.Copy).then_inc(lev_out_a.sem, 1)
            for w in range(2):
                act.wait_ge(qkT_done.sem, qkT_done.at(l, 2 * w + 1))
                act.activation(qkT[:, w, :, tok(0)], bank_view((2, 0)[w]), ACT.Copy).then_inc(qkT_out_a.sem, 1)

            def softmax_exp(t, heads):
                for h in heads:
                    bank, at = s_bank(t, h)
                    keys = (t + 1) * P
                    ins = act.activation((p0, p1)[t][:, h, :], ps[:, bank, at:at + keys], ACT.Exp, bias=nb[:, t, h:h + 1],
                                         scale=scl[:, t, h:h + 1], accum_out=rows[:, t, h:h + 1])
                ins.then_inc(exp_done.sem, 1)

            act.wait_ge(nb_ready.sem, nb_ready.at(l, 1))
            softmax_exp(0, range(8))
            act.wait_ge(ho_done.sem, ho_done.at(l, 1))
            act.activation(osq[:, :], ps[:, 1, :], ACT.Square).then_inc(hsq_ready.sem, 1)
            act.wait_ge(dT_done.sem, dT_done.at(l, 1))
            act.activation(dT[:, :, :].rearrange("p g t -> p (g t)"), ps[:, 0, :], ACT.Copy).then_inc(dT_out.sem, 1)
            act.wait_ge(yhT_done.sem, yhT_done.at(l, 1))
            act.activation(hT_hi[:, 6:8, :].rearrange("p g t -> p (g t)"), ps[:, 1, :], ACT.Copy).then_inc(yh_hi.sem, 1)
            act.wait_ge(nb_ready.sem, nb_ready.at(l, 2))
            softmax_exp(1, range(0, 4))
            act.wait_ge(yp_done.sem, yp_done.at(l, 1))
            for g in range(2):
                ins = act.activation(hT_hi[:, 4 + g, :], ps[:, 0, g * SEQ:(g + 1) * SEQ], ACT.Copy,
                                     scale=pscale_now[:, g:g + 1])
            ins.then_inc(yp_hi.sem, 1)

            def probs_out(n):
                act.wait_ge(pT_done.sem, pT_done.at(l, n + 1))
                if n > 0:
                    act.wait_ge(pv_done.sem, pv_done.at(l, n))
                act.activation(pT[:, 0, :], ps[:, 4, :], ACT.Copy).then_inc(pT_a.sem, 1)

            probs_out(0)
            act.wait_ge(nb_ready.sem, nb_ready.at(l, 3))
            softmax_exp(1, range(4, 8))
            split_block(split_hi, act, l, B_OUT + 1)
            probs_out(1)
            probs_out(2)
            for t in range(TILES):
                act.wait_ge(yaT_done.sem, yaT_done.at(l, t + 1))
                act.activation(hT_hi[:, 0:4, tok(t)], bank_view(t), ACT.Copy).then_inc(ya_hi.sem, 1)

        def mix_vector(dve, chain, l):
            dve.wait_ge(consts_in.sem, 16 * N_CONSTS)
            split_block(split_lo, dve, l, B_IN + 1)
            split_block(split_lo, dve, l, B_IN + 2)
            dve.wait_ge(sig_ready.sem, sig_ready.at(l, 1))
            for ft in range(2):
                cols = slice(ft * SEQ, (ft + 1) * SEQ)
                ins = dve.tensor_scalar(fsig[:, cols], fsig[:, cols], oml_now[:, ft:ft + 1], lbf_now[:, ft:ft + 1],
                                        ALU.mult, ALU.add)
            chain.step(ins)
            chain.step(dve.tensor_scalar(small[:, :], fsig[:, :], 2.0 ** -32, None, ALU.is_lt))
            chain.step(dve.tensor_scalar(dec[:, 0, :], small[:, :], 2.0 ** LN_SHIFT - 1.0, 1.0, ALU.mult, ALU.add))
            dve.tensor_tensor(fsig[:, :], fsig[:, :], dec[:, 0, :], ALU.mult).then_inc(f_ready.sem, 1)
            dve.wait_ge(sig_ready.sem, sig_ready.at(l, 2))
            for ft in range(2):
                cols = slice(ft * SEQ, (ft + 1) * SEQ)
                dve.tensor_scalar(key[:, cols], key[:, cols], oml_now[:, ft:ft + 1], None, ALU.mult)
            dve.scalar_tensor_tensor(qry[:, :], ps[:, TR, :], HD ** -0.5, qry[:, :], ALU.mult,
                                     ALU.mult).then_inc(kq_ready.sem, 1)
            dve.wait_ge(ln_ready.sem, ln_ready.at(l, 1))
            chain.step(dve.scalar_tensor_tensor(fsig[:, :], small[:, :], -LN_SHIFT * float(np.log(2.0)), fsig[:, :],
                                                ALU.mult, ALU.add))
            dve.tensor_tensor_scan(pc[:, :], scan_keep[:, :], fsig[:, :], 0.0, ALU.mult, ALU.add).then_inc(pc_ready.sem, 1)
            split_block(split_lo, dve, l, B_IN + 3)
            dve.wait_ge(clear_done.sem, clear_done.at(l, 1))

            def level_take(v):
                dve.wait_ge(lev_done.sem, lev_done.at(l, v + 1))
                plain_wait(dve)
                for par in range(2):
                    ins = dve.copy_predicated(sp[:, 4 * par:4 * par + 4, :], bc(levmask[:, v, :], 1, [P, 4, 64]),
                                              bank_view(TR + par, 0, 256, 64))
                ins.then_inc(lev_out.sem, 1)

            def level_factors(v):
                b = LEVELS[v]
                dve.wait_ge(dec_ready.sem, dec_ready.at(l, v))
                if v >= 3:
                    dve.wait_ge(lev_done.sem, lev_done.at(l, v - 1))
                fl, fr = level_halves(dec[:, v % 2, :], b)
                dve.scalar_tensor_tensor(level_halves(kl[:, v % 2, :], b)[0], fl, 1.0, level_halves(key[:, :], b)[0],
                                         ALU.min, ALU.mult)
                dve.scalar_tensor_tensor(level_halves(ql[:, v % 2, :], b)[1], fr, 1.0, level_halves(qry[:, :], b)[1],
                                         ALU.min, ALU.mult).then_inc(kq_ready.sem, 1)

            def head_squares(n):
                nh = 8
                dve.wait_ge(hsq_ready.sem, hsq_ready.at(l, n + 1))
                dve.tensor_reduce(hss[:, n, 0:nh], osq[:, :].rearrange("p (h d) -> p h d", d=HD), AX,
                                  ALU.add).then_inc(hsum_done.sem, 1)
                dve.wait_ge(hsum_done.sem, hsum_done.at(l, n + 1))
                dve.tensor_scalar(hvar[:, n, 0:nh], hss[:, n, 0:nh], 1.0 / HD, EPS, ALU.mult,
                                  ALU.add).then_inc(hvar_ready.sem, 1)

            for part in (QA, KA, VA, UP):
                for t in range(TILES):
                    v = 2 * (part - QA) + t
                    if v > 0:
                        level_take(v - 1)
                    level_factors(v + 1)
                    if part in (QA, KA):
                        head_squares(2 * (part - QA) + t)
                    if part < UP:
                        split_lo(dve, l, B_IN + part + 2, t, unit_cols(B_IN + part + 2))
            for w in range(2):
                dve.wait_ge(qkT_done.sem, qkT_done.at(l, 2 * w + 2))
                dve.tensor_copy(qkT[:, w, :, tok(1)], bank_view((3, 1)[w])).then_inc(qkT_out_v.sem, 1)

            for t in range(TILES):
                dve.wait_ge(hrs_ready.sem, hrs_ready.at(l, t + 1))
                dve.tensor_scalar(scl[:, t, :], hrs[:, t, :], HD ** -0.5, None, ALU.mult)

            def softmax_bias(n):
                t, heads = (0, slice(0, 8)) if n == 0 else (1, slice(4 * n - 4, 4 * n))
                dve.wait_ge(s_done.sem, s_done.at(l, n + 1))
                keys = (t + 1) * P
                for par in range(2):
                    first = heads.start + par
                    dve_in = bank_view(s_bank(t, first)[0], 0, 512, keys)
                    ins = dve.tensor_reduce(mx[:, t, first:heads.stop:2], dve_in, AX, ALU.max)
                chain.step(ins)
                dve.scalar_tensor_tensor(nb[:, t, heads], mx[:, t, heads], -1.0, scl[:, t, heads], ALU.mult,
                                         ALU.mult).then_inc(nb_ready.sem, 1)

            softmax_bias(0)

            head_squares(4)
            dve.wait_ge(hrs_ready.sem, hrs_ready.at(l, 5))
            dve.wait_ge(gate_done.sem, gate_done.at(l, 1))
            hv = "p (h d) -> p h d"
            chain.step(dve.tensor_tensor(osq[:, :].rearrange(hv, d=HD), ps[:, 1, :].rearrange(hv, d=HD),
                                         bc(hrs[:, 4, :], 2, [P, 8, HD]), ALU.mult))
            dve.tensor_tensor(osq[:, :], osq[:, :], gs[:, :], ALU.mult).then_inc(yh_ready.sem, 1)

            softmax_bias(1)
            dve.wait_ge(yh_hi.sem, yh_hi.at(l, 1))
            dve.tensor_tensor(hT_lo[:, 6:8, :].rearrange("p g t -> p (g t)"), ps[:, 1, :],
                              hT_hi[:, 6:8, :].rearrange("p g t -> p (g t)").bitcast(F32),
                              ALU.subtract).then_inc(yh_lo.sem, 1)
            dve.wait_ge(yp_hi.sem, yp_hi.at(l, 1))
            for g in range(2):
                ins = dve.scalar_tensor_tensor(hT_lo[:, 4 + g, :], ps[:, 0, g * SEQ:(g + 1) * SEQ], pscale_now[:, g:g + 1],
                                               hT_hi[:, 4 + g, :].bitcast(F32), ALU.mult, ALU.subtract)
            ins.then_inc(yp_lo.sem, 1)

            softmax_bias(2)

            def probs_out(n):
                dve.wait_ge(pT_done.sem, pT_done.at(l, n + 1))
                if n > 0:
                    dve.wait_ge(pv_done.sem, pv_done.at(l, n))
                dve.tensor_copy(pT[:, 1, :], ps[:, 5, :]).then_inc(pT_v.sem, 1)

            probs_out(0)

            def attention_rows(t):
                dve.wait_ge(exp_done.sem, exp_done.at(l, 1 + 2 * t))
                chain.step(dve.reciprocal(rinv[:, t, :], rows[:, t, :]))
                dve.wait_ge(pv_done.sem, pv_done.at(l, 1 + 2 * t))
                dve.tensor_tensor(ya[:, t, :].rearrange(hv, d=HD), ps[:, t, :].rearrange(hv, d=HD),
                                  bc(rinv[:, t, :], 2, [P, 8, HD]), ALU.mult).then_inc(ya_ready.sem, 1)

            def attention_lo(t):
                dve.wait_ge(ya_hi.sem, ya_hi.at(l, t + 1))
                dve.tensor_tensor(hT_lo[:, 0:4, tok(t)], bank_view(t), hT_hi[:, 0:4, tok(t)].bitcast(F32),
                                  ALU.subtract).then_inc(ya_lo.sem, 1)

            attention_rows(0)
            split_block(split_lo, dve, l, B_OUT + 1)
            probs_out(1)
            probs_out(2)
            attention_lo(0)
            attention_rows(1)
            attention_lo(1)

        def mix_pool(pool, chain, l):
            pool.wait_ge(unit_used.sem, unit_used.at(l, 2 * B_IN))
            plain_wait(pool)
            pool.memset(kl[:, :, :], 0.0)
            pool.memset(ql[:, :, :], 0.0)
            pool.memset(sp[:, :, :], 0.0)
            pool.memset(st[:, :, :], 0.0).then_inc(clear_done.sem, 1)
            pool.wait_ge(clear_done.sem, clear_done.at(l, 1))
            pool.wait_ge(gsig_ready.sem, gsig_ready.at(l, 1))
            g3 = gs[:, :].rearrange("p (t c) -> p t c", t=2)
            chain.step(pool.tensor_tensor(g3, g3, ig[:, :, 256:512], ALU.mult))
            gh = gs[:, :].rearrange("p (h d) -> p h d", d=HD)
            pool.tensor_tensor(gh, gh, rgain[:, bass.ds(l, 1), 4, :].to_broadcast([P, 8, HD]), ALU.mult).then_inc(gate_done.sem, 1)
            pool.wait_ge(pc_ready.sem, pc_ready.at(l, 1))

            def level_difference(v):
                b = LEVELS[v]
                if v >= 3:
                    pool.wait_ge(kq_ready.sem, kq_ready.at(l, v - 1))
                src = pc[:, :].rearrange("p (n j) -> p n j", j=2 * b)
                dst = dec[:, v % 2, :].rearrange("p (n j) -> p n j", j=2 * b)
                if b < P:
                    ref = src[:, :, b - 1:b].to_broadcast([P, 2 * SEQ // (2 * b), 2 * b])
                    pool.tensor_tensor(dst, src, ref, ALU.subtract).then_inc(dif_ready.sem, 1)
                else:
                    ref = src[:, :, b - 1:b].to_broadcast([P, 2, b])
                    pool.tensor_tensor(dst[:, :, 0:b], src[:, :, 0:b], ref, ALU.subtract)
                    pool.tensor_copy(dst[:, :, b:2 * b], src[:, :, b:2 * b]).then_inc(dif_ready.sem, 1)

            def head_rstd(n):
                pool.wait_ge(hvar_ready.sem, hvar_ready.at(l, n + 1))
                pool.tensor_tensor(hrs[:, n, :], hvar[:, n, :], halfneg[:, :], ALU.pow).then_inc(hrs_ready.sem, 1)

            def rotate(w, t):
                part = QA + w
                head_rstd(2 * w + t)
                pool.wait_ge(proj_out.sem, proj_out.at(l, 2 * part + t + 1))
                z = qk[:, w, t, :].rearrange("p (h d) -> p h d", d=HD)
                tmp = rtmp[:, :].rearrange("p (h d) -> p h d", d=HD)
                cos, sin = rope_now[:, t, 2 * w, :], rope_now[:, t, 2 * w + 1, :]
                if w == 1:
                    pool.wait_ge(hrs_ready.sem, hrs_ready.at(l, 2 * w + t + 1))
                    chain.step(pool.tensor_tensor(z, z, bc(hrs[:, 2 + t, :], 2, [P, 8, HD]), ALU.mult))
                q = HD // 2
                pool.tensor_tensor(tmp[:, :, 0:q], z[:, :, q:HD], bc(sin[:, 0:q], 1, [P, 8, q]), ALU.mult)
                chain.step(pool.tensor_tensor(tmp[:, :, q:HD], z[:, :, 0:q], bc(sin[:, q:HD], 1, [P, 8, q]), ALU.mult))
                chain.step(pool.tensor_tensor(z, z, bc(cos, 1, [P, 8, HD]), ALU.mult))
                pool.tensor_tensor(z, z, tmp, ALU.add).then_inc(rope_ready.sem, 1)
                pool.wait_ge(rope_ready.sem, rope_ready.at(l, 2 * w + t + 1))

            level_difference(1)
            level_difference(2)
            level_difference(3)
            rotate(0, 0)
            level_difference(4)
            rotate(0, 1)
            level_difference(5)
            rotate(1, 0)
            level_difference(6)
            level_difference(7)
            rotate(1, 1)
            level_difference(8)
            pool.wait_ge(lev_out.sem, lev_out.at(l, PACKED))
            pool.wait_ge(dif_ready.sem, dif_ready.at(l, 8))
            for c in range(2):
                if c == 1:
                    pool.wait_ge(st_ready.sem, st_ready.at(l, 1))
                plain_wait(pool)
                r = slice(64 * c, 64 * c + 64)
                pool.tensor_copy(st[r, :, 64 * c:64 * c + 64], sp[r, :, :]).then_inc(st_ready.sem, 1)
            pool.wait_ge(st_ready.sem, st_ready.at(l, 2))
            head_rstd(4)

        oml_now, _ = place("oml_now", [P, 2], at=None)
        lbf_now, _ = place("lbf_now", [P, 2])
        pscale_now, _ = place("pscale_now", [P, 2])
        rope_now, _ = place("rope_now", [P, TILES, 4, HD])
        pool_now, _ = place("pool_now", [P, 2, P])
        assert cursor[0] <= nc.sbuf_usable_end, cursor[0] - nc.sbuf_usable_end
        layer_ready = signal("layer_ready", 4)
        poolw_in = signal("poolw_in", 4 * 16)

        def layer_tables(pool, l):
            pool.wait_ge(consts_in.sem, 16 * N_CONSTS)
            pool.wait_ge(ready_v.sem, 1)
            pool.wait_ge(unit_used.sem, unit_used.at(l, 0))
            plain_wait(pool)
            for dst, src in ((oml_now, oml), (lbf_now, lbf), (pscale_now, lbin[:, 1])):
                pool.tensor_copy(dst[:, :], src[:, bass.ds(l, 1), :].rearrange("p o c -> p (o c)")).then_inc(
                    layer_ready.sem, 1)
            for k in range(4):
                for t in range(TILES):
                    ins = pool.tensor_tensor(rope_now[:, t, k, :], trig[:, t, k % 2, :],
                                             rgain[:, bass.ds(l, 1), k, :].rearrange("p o d -> p (o d)"), ALU.mult)
            ins.then_inc(layer_ready.sem, 1)
            pool.wait_ge(layer_ready.sem, layer_ready.at(l, 4))
            for g in range(4):
                r = slice(64 * (g % 2), 64 * (g % 2) + 64)
                pool.dma_start(pool_now[r, g // 2, r],
                               a["pool_w"][bass.ds(l, 1), g].rearrange("o c e -> (o c) e")).then_inc(poolw_in.sem, 16)

        block = ctx.enter_context(nc.Block())

        @block.sync
        def _(sp_):
            for t in range(TILES):
                sp_.dma_start(x[:, t, :], a["x"][0, tok(t), :]).then_inc(x_in[t].sem, 16)
                if t == 0:
                    sp_.dma_start(ident[:, :], a["c_ident"]).then_inc(ident_in.sem, 16)

            def load_gain(l, n, name):
                if n > 0:
                    sp_.wait_ge(xn_ready.sem, xn_ready.at(l, 2 * n))
                plain_wait(sp_)
                src = a[name][bass.ds(l, 1), :]
                sp_.dma_start(gain[:, :], src.to_broadcast([P, D])).then_inc(gain_in.sem, 16)

            def gate_up(l, f, c, h, pair=0):
                wg, wu = (("ffn1_w_gate", "ffn1_w_up"), ("ffn2_w_gate", "ffn2_w_up"))[f]

                def src(dst):
                    d = dst.rearrange("p (k g c) -> p k g c", k=4, g=2)
                    for g, name in enumerate((wg, wu)):
                        v = a[name][bass.ds(l, 1), h * 512:(h + 1) * 512, bass.ds(c * CHUNK + pair * (2 * CHUNK), CHUNK)]
                        yield d[:, :, g, :], v.rearrange("o (k p) c -> p (o k) c", p=P)
                return src

            def rows_of(l, name, first, per, width, col=0):
                def src(dst):
                    d = dst.rearrange("p (k c) -> p k c", k=per)
                    for g in range(2):
                        if per > 1:
                            k0, n, c0, wd = g * per // 2, per // 2, 0, width
                        else:
                            k0, n, c0, wd = 0, 1, g * width // 2, width // 2
                        v = a[name][bass.ds(l, 1), first + k0 * P:first + (k0 + n) * P, col + c0:col + c0 + wd]
                        yield d[:, k0:k0 + n, c0:c0 + wd], v.rearrange("o (k p) c -> p (o k) c", p=P)
                return src

            def load_ffn(l, f):
                b0, bd = (B_FFN1, B_FFN2)[f], (B_DOWN1, B_DOWN2)[f]
                for h in range(2):
                    load_unit(sp_, l, b0, h, gate_up(l, f, 0, h), UNIT)
                with chunk_pairs(sp_) as i:
                    for e in range(2):
                        for h in range(2):
                            load_unit(sp_, l, b0 + 1 + e, h, gate_up(l, f, 1 + e, h, i), UNIT, i)
                if f == 0:
                    load_gain(l, 1, "mix_norm")
                name = ("ffn1_w_down", "ffn2_w_down")[f]
                for j in range(DOWN):
                    cols = unit_cols(bd + j)
                    per = cols // D
                    for h in range(2):
                        load_unit(sp_, l, bd + j, h, rows_of(l, name, (4 * j + h * per) * P, per, D), cols)

            with sp_.Fori(0, DEPTH) as l:
                sp_.wait_ge(xn_ready.sem, xn_ready.at(l, 0))
                load_gain(l, 0, "ffn1_norm")
                load_ffn(l, 0)
                for part, (col, width) in enumerate(IN_COLS):
                    for h in range(2):
                        load_unit(sp_, l, B_IN + part, h, rows_of(l, "w_in", h * 512, 4, width, col), 4 * width)
                load_gain(l, 2, "ffn2_norm")
                for j in range(2):
                    for h in range(2):
                        load_unit(sp_, l, B_OUT + j, h, rows_of(l, "w_out", (512 if j == 0 else 0) + h * 256, 2, D), UNIT)
                load_ffn(l, 1)
            for t in range(TILES):
                sp_.wait_ge(resid.sem, 12 + (DEPTH - 1) * 12 + 8 + 2 * t + 2)
                sp_.dma_start(out[0, tok(t), :], x[:, t, :]).then_inc(out_done.sem, 16)
            sp_.wait_ge(out_done.sem, 32)

        @block.gpsimd
        def _(pool):
            pool.memset(halfneg[:, :], -0.5)
            pool.memset(pool_now[:, :, :], 0.0)
            pool.memset(lbt[:, :, :], 0.0).then_inc(poolw_zero.sem, 1)
            pool.wait_ge(poolw_zero.sem, 1)
            pool.dma_start(lbin[:, :, :, :], a["feature_rows"]).then_inc(lb_in.sem, 16)
            pool.dma_start(rgain[:, :, :, :], a["head_gains"].to_broadcast([P, DEPTH, 5, HD])).then_inc(consts_in.sem, 16)
            for dst, name in ((trig, "c_trig"), (levmask, "c_levels"), (ident16, "c_ident16"), (causal16, "c_causal"),
                              (scan_keep, "c_keep"), (band0, "c_band0"), (band1, "c_band1")):
                idx_ = tuple(slice(None) for _ in a[name].shape)
                dst = dst[idx_].bitcast(U16) if name in BITS16 else dst[idx_]
                pool.dma_start(dst, a[name]).then_inc(consts_in.sem, 16)
            for t in range(TILES):
                pool.wait_ge(x_in[t].sem, 16)
                pool.sem_inc(resid.sem, 8 + 2 if t == 0 else 2)
            with pool.Fori(0, DEPTH) as l:
                chain = Chain(pchain, pool, l)
                for n in range(3):
                    for t in range(TILES):
                        norm_rstd(pool, l, n, t)
                    if n == 0:
                        layer_tables(pool, l)
                    elif n == 1:
                        mix_pool(pool, chain, l)
                assert chain.n == P_STEPS, chain.n

        @block.scalar
        def _(act):
            act.wait_ge(lb_exp.sem, 1)
            act.activation(lbe[:, 0:4], lbe[:, 0:4], ACT.Exp).then_inc(lb_exp.sem, 1)
            with act.Fori(0, DEPTH) as l:
                norm_squares(act, l, 0, 0)
                split_hi(act, l, 0, 0)
                norm_hi(act, l, 0, 0, TR)
                norm_squares(act, l, 0, 1)
                split_hi(act, l, 0, 1)
                norm_hi(act, l, 0, 1, TR)
                ffn_side(act, l, 0, split_hi, chunk_gate, chunk_hi)
                norm_tail_scalar(act, l, 1, B_IN, TR)
                mix_scalar(act, l)
                norm_tail_scalar(act, l, 2, B_FFN2, 4)
                ffn_side(act, l, 1, split_hi, chunk_gate, chunk_hi)

        @block.vector
        def _(dve):
            dve.sem_inc(lo_ready.sem, RAW)
            dve.sem_inc(prod_ready.sem, 2)
            dve.sem_inc(alo_ready.sem, 2)
            dve.sem_inc(xn_ready.sem, 6)
            dve.wait_ge(lb_in.sem, 16)
            vsteps = [0]

            def link(ins):
                vsteps[0] += 1
                ins.then_inc(setup_v.sem, 1)
                dve.wait_ge(setup_v.sem, vsteps[0])

            link(dve.tensor_tensor(lbe[:, 4:6], lbin[:, 0, 0, :], lbin[:, 0, 1, :], ALU.max))
            dve.tensor_tensor(lbe[:, 0:2], lbin[:, 0, 0, :], lbe[:, 4:6], ALU.subtract)
            link(dve.tensor_tensor(lbe[:, 2:4], lbin[:, 0, 1, :], lbe[:, 4:6], ALU.subtract))
            dve.sem_inc(lb_exp.sem, 1)
            dve.wait_ge(lb_exp.sem, 2)
            link(dve.tensor_tensor(lbe[:, 4:6], lbe[:, 0:2], lbe[:, 2:4], ALU.add))
            link(dve.reciprocal(lbe[:, 6:8], lbe[:, 4:6]))
            link(dve.tensor_tensor(lbt[:, 1, :], lbe[:, 0:2], lbe[:, 6:8], ALU.mult))
            link(dve.tensor_scalar(lbf[:, :, :], lbt[:, :, :], LB_FLOOR, None, ALU.max))
            link(dve.tensor_scalar(oml[:, :, :], lbt[:, :, :], -1.0, 1.0, ALU.mult, ALU.add))
            dve.sem_inc(ready_v.sem, 1)
            with dve.Fori(0, DEPTH) as l:
                chain = Chain(vchain, dve, l)
                norm_rows(dve, chain, l, 0, 0)
                split_lo(dve, l, 0, 0)
                norm_lo(dve, l, 0, 0, TR)
                split_lo(dve, l, 0, 1)
                norm_rows(dve, chain, l, 0, 1)
                norm_lo(dve, l, 0, 1, TR)
                ffn_side(dve, l, 0, split_lo, chunk_product, chunk_lo)
                dve.wait_ge(layer_ready.sem, layer_ready.at(l, 4))
                norm_tail_vector(dve, chain, l, 1, B_IN, TR, DN_FFN, 0.5)
                mix_vector(dve, chain, l)
                norm_tail_vector(dve, chain, l, 2, B_FFN2, 4, DN_MIX, 1.0)
                ffn_side(dve, l, 1, split_lo, chunk_product, chunk_lo)
                for t in range(TILES):
                    add_residual(dve, l, 2, t, DN_FFN, 0.5)
                assert chain.n == V_STEPS, chain.n

        @block.tensor
        def _(pe):
            pe.sem_inc(unit_used.sem, 4)
            pe.wait_ge(ident_in.sem, 16)
            with pe.Fori(0, DEPTH) as l:
                norm_transpose(pe, l, 0, 0, TR)
                ffn_tensor(pe, l, 0)
                mix_tensor(pe, l)
                ffn_tensor(pe, l, 1)


V_STEPS = 16
P_STEPS = 11
BITS16 = ("c_ident16", "c_causal", "c_keep")
N_CONSTS = 8


def constants():
    def bits16(table):
        return (np.ascontiguousarray(table, dtype=np.float32).view(np.uint32) >> 16).astype(np.uint16)

    tok = np.arange(SEQ)
    inv = THETA ** (-np.arange(HD // 2, dtype=np.float32) / np.float32(HD // 2))
    ang = (tok.astype(np.float32)[:, None] * inv[None, :].astype(np.float32)).astype(np.float32)
    cos, sin = np.cos(ang), np.sin(ang)
    trig = np.stack([np.concatenate([cos, cos], 1), np.concatenate([-sin, sin], 1)], 1)
    trig = trig.reshape(TILES, P, 2, HD).transpose(1, 0, 2, 3).astype(np.float32)
    s, t = np.arange(64)[:, None], np.arange(64)[None, :]
    levels = []
    for b in LEVELS[:PACKED]:
        if b == 0:
            m = s == t
        else:
            m = (s // (2 * b) == t // (2 * b)) & (s % (2 * b) < b) & (t % (2 * b) >= b)
        levels.append(m)
    levels = np.tile(np.stack(levels, 1).astype(np.int32), (2, 1, 1))
    band = np.zeros((len(POOL_WINDOWS), SEQ, SEQ), np.float64)
    for g, w in enumerate(POOL_WINDOWS):
        for q in range(SEQ):
            lo = max(0, q + 1 - w)
            band[g, lo:q + 1, q] = 1.0 / min(q + 1, w)
            band[g, q, q] -= 1.0
    keep = (np.arange(2 * SEQ) % P != 0)
    q, k = np.arange(P)[:, None], np.arange(P)[None, :]
    return {
        "c_ident": np.eye(P, dtype=np.float32),
        "c_ident16": bits16(np.eye(P)),
        "c_causal": bits16(np.where(k <= q, 0.0, NEG)),
        "c_trig": trig,
        "c_levels": levels,
        "c_keep": bits16(np.broadcast_to(keep, (P, 2 * SEQ))),
        "c_band0": np.ascontiguousarray(band[:, :P, :BAND0].transpose(1, 0, 2)).astype(np.float32),
        "c_band1": np.ascontiguousarray(band[:, P:, P:].transpose(1, 0, 2)).astype(np.float32),
    }


def small_operands(arrays):
    q, k, o = (arrays.pop(name) for name in ("q_norm", "k_norm", "hgrn_out_norm"))
    swapped = [np.concatenate([g[:, HD // 2:], g[:, :HD // 2]], 1) for g in (q, k)]
    gains = np.stack([q, swapped[0], k, swapped[1], o], 1)[None]
    rows = np.stack([arrays.pop(name) for name in ("hgrn_lb", "pool_scale")])
    rows = rows.reshape(2, DEPTH, 2, P).transpose(3, 0, 1, 2)
    return {"head_gains": np.ascontiguousarray(gains), "feature_rows": np.ascontiguousarray(rows)}


def kernel(**inputs):
    import concourse.bacc as bacc
    from concourse.bass_utils import run_bass_kernel_spmd

    nc = bacc.Bacc("TRN2", target_bir_lowering=False, num_devices=1)
    arrays = {name: np.ascontiguousarray(v) for name, v in inputs.items()}
    arrays.update(constants())
    arrays.update(small_operands(arrays))
    args = {name: nc.dram_tensor(name, v.shape, mybir.dt.from_np(v.dtype), kind="ExternalInput").ap()
            for name, v in arrays.items()}
    out = nc.dram_tensor("out", (1, SEQ, D), F32, kind="ExternalOutput").ap()
    build(nc, args, out)
    return run_bass_kernel_spmd(nc, [arrays], core_ids=[0]).results[0]["out"]
```
